# Optimizing a Trainium2 kernel written in Bass

```python
import math
import jax, jax.numpy as jnp
from jax import lax
import numpy as np

D_MODEL = 2048
BATCH = 1
SEQ = 512
DEPTH = 2
DEC_BATCH = 8
DEC_SEQ = 4
PAST_LEN = 1024
PAGE_SIZE = 128

N_A_LAYERS = DEPTH // 2
N_B_LAYERS = DEPTH - N_A_LAYERS
D_RNN = (D_MODEL * 5) // 4
LRU_BLOCK = 256
N_LRU_BLOCKS = D_RNN // LRU_BLOCK
CONV_W = 4
LRU_C = 8.0
HEAD_DIM = 128
N_HEADS = D_MODEL // HEAD_DIM
KV_HEADS = 4
GROUP = N_HEADS // KV_HEADS
ATT_WIDTH = N_HEADS * HEAD_DIM
KV_WIDTH = KV_HEADS * HEAD_DIM
Q_BLOCK = 128
LOGIT_BIAS_INIT = -8.0
EPS = 1e-6

kernel_name = "yoco_rglru_stickbreaking_step"

def rms_norm(x, g):
    xf = x.astype(jnp.float32)
    y = xf * lax.rsqrt(jnp.mean(xf * xf, axis=-1, keepdims=True) + EPS)
    return (y * g.astype(jnp.float32)).astype(x.dtype)

def rglru_mixer(u, conv_buf, h0, w_in, conv_w, conv_b, w_r, b_r, w_i, b_i, lam, w_out):
    B, T, _ = u.shape
    proj = u @ w_in
    xr, gate = proj[..., :D_RNN], proj[..., D_RNN:]
    xpad = jnp.concatenate([conv_buf.astype(xr.dtype), xr], axis=1)
    xc = conv_b + xpad[:, 0:T] * conv_w[0]
    for k in range(1, CONV_W):
        xc = xc + xpad[:, k:k + T] * conv_w[k]
    new_buf = xpad[:, T:]
    xb = xc.reshape(B, T, N_LRU_BLOCKS, LRU_BLOCK)
    r = jax.nn.sigmoid(jnp.einsum('btnc,ncd->btnd', xb, w_r).reshape(B, T, D_RNN) + b_r)
    i = jax.nn.sigmoid(jnp.einsum('btnc,ncd->btnd', xb, w_i).reshape(B, T, D_RNN) + b_i)
    log_a = -LRU_C * r.astype(jnp.float32) * jax.nn.softplus(-lam.astype(jnp.float32))
    a = jnp.exp(log_a)
    b = jnp.sqrt(-jnp.expm1(2.0 * log_a)) * (i * xc).astype(jnp.float32)

    def step(h, ab):
        a_t, b_t = ab
        h = a_t * h + b_t
        return h, h

    h_last, hs = lax.scan(step, h0.astype(jnp.float32),
                          (jnp.swapaxes(a, 0, 1), jnp.swapaxes(b, 0, 1)))
    y = jnp.swapaxes(hs, 0, 1).astype(u.dtype) * jax.nn.silu(gate)
    return y @ w_out, new_buf, h_last

def stick_breaking_block(qb, qpos, k, v, kpos, bias):
    z = jnp.einsum('bqkgd,bskd->bkgqs', qb, k).astype(jnp.float32) / math.sqrt(HEAD_DIM)
    z = z + bias.astype(jnp.float32)[None, :, :, None, None]
    mask = kpos[None, :] < qpos[:, None]
    log_keep = jnp.where(mask, jax.nn.log_sigmoid(-z), 0.0)
    suffix = lax.cumsum(log_keep, axis=4, reverse=True) - log_keep
    attn = jnp.where(mask, jnp.exp(jax.nn.log_sigmoid(z) + suffix), 0.0)
    o = jnp.einsum('bkgqs,bskd->bqkgd', attn.astype(v.dtype), v)
    return o.reshape(qb.shape[0], qb.shape[1], ATT_WIDTH)

def stick_breaking_mixer(u, k, v, q_pos, k_pos, w_in, bias, w_out):
    B, T, _ = u.shape
    proj = u @ w_in
    q, gate = proj[..., :ATT_WIDTH], proj[..., ATT_WIDTH:]
    qb_len = min(Q_BLOCK, T)
    n_blk = T // qb_len
    qs = q.reshape(B, n_blk, qb_len, KV_HEADS, GROUP, HEAD_DIM).transpose(1, 0, 2, 3, 4, 5)
    ps = q_pos.reshape(n_blk, qb_len)
    bias_g = bias.reshape(KV_HEADS, GROUP)
    o = lax.map(lambda a: stick_breaking_block(a[0], a[1], k, v, k_pos, bias_g), (qs, ps))
    o = jnp.swapaxes(o, 0, 1).reshape(B, T, ATT_WIDTH)
    return (o * jax.nn.silu(gate)) @ w_out

def run_group(x, conv_state, h_state, past_k, past_v, g_pre, g_post, a_w_in, a_conv_w, a_conv_b,
              a_w_r, a_b_r, a_w_i, a_b_i, a_lambda, a_w_out, kv_norm, w_k, w_v, b_w_in, b_logit, b_w_out):
    B, T, _ = x.shape
    P = past_k.shape[1]
    q_pos = P + jnp.arange(T, dtype=jnp.int32)
    k_pos = jnp.arange(P + T, dtype=jnp.int32)
    new_bufs, new_hs = [], []
    k_new = v_new = k_all = v_all = None
    for layer in range(DEPTH):
        u = rms_norm(x, g_pre[layer])
        if layer < N_A_LAYERS:
            out, buf, hl = rglru_mixer(u, conv_state[:, layer], h_state[:, layer], a_w_in[layer],
                                       a_conv_w[layer], a_conv_b[layer], a_w_r[layer], a_b_r[layer],
                                       a_w_i[layer], a_b_i[layer], a_lambda[layer], a_w_out[layer])
            new_bufs.append(buf)
            new_hs.append(hl)
        else:
            j = layer - N_A_LAYERS
            out = stick_breaking_mixer(u, k_all, v_all, q_pos, k_pos, b_w_in[j], b_logit[j], b_w_out[j])
        x = x + rms_norm(out, g_post[layer])
        if layer == N_A_LAYERS - 1:
            s = rms_norm(x, kv_norm)
            k_new = (s @ w_k).reshape(B, T, KV_HEADS, HEAD_DIM)
            v_new = (s @ w_v).reshape(B, T, KV_HEADS, HEAD_DIM)
            k_all = jnp.concatenate([past_k.astype(k_new.dtype), k_new], axis=1)
            v_all = jnp.concatenate([past_v.astype(v_new.dtype), v_new], axis=1)
    return x, jnp.stack(new_bufs, axis=1), jnp.stack(new_hs, axis=1), k_new, v_new

def setup_inputs(seed: int = 0) -> dict:
    key = jax.random.key(seed)
    ks = jax.random.split(key, 24)
    f32 = jnp.float32
    n_pages = PAST_LEN // PAGE_SIZE
    n_used = DEC_BATCH * n_pages
    n_phys = n_used + max(1, n_used // 4)
    nrm = lambda k, shape, s: jax.random.normal(k, shape, f32) * s
    x_prompt = nrm(ks[0], (BATCH, SEQ, D_MODEL), 1.0)
    x_sample = nrm(ks[1], (DEC_BATCH, DEC_SEQ, D_MODEL), 1.0)
    cache_k = nrm(ks[2], (n_phys, PAGE_SIZE, KV_HEADS, HEAD_DIM), 1.0)
    cache_v = nrm(ks[3], (n_phys, PAGE_SIZE, KV_HEADS, HEAD_DIM), 1.0)
    state_conv = nrm(ks[4], (DEC_BATCH, N_A_LAYERS, CONV_W - 1, D_RNN), 1.0)
    state_h = nrm(ks[5], (DEC_BATCH, N_A_LAYERS, D_RNN), 0.5)
    page_table = jax.random.permutation(ks[6], n_phys)[:n_used].astype(jnp.int32).reshape(DEC_BATCH, n_pages)
    g_pre = 1.0 + nrm(ks[7], (DEPTH, D_MODEL), 0.05)
    g_post = 1.0 + nrm(ks[8], (DEPTH, D_MODEL), 0.05)
    a_w_in = nrm(ks[9], (N_A_LAYERS, D_MODEL, 2 * D_RNN), D_MODEL ** -0.5)
    a_conv_w = nrm(ks[10], (N_A_LAYERS, CONV_W, D_RNN), CONV_W ** -0.5)
    a_conv_b = nrm(ks[11], (N_A_LAYERS, D_RNN), 0.01)
    a_w_r = nrm(ks[12], (N_A_LAYERS, N_LRU_BLOCKS, LRU_BLOCK, LRU_BLOCK), LRU_BLOCK ** -0.5)
    a_b_r = nrm(ks[13], (N_A_LAYERS, D_RNN), 0.01)
    a_w_i = nrm(ks[14], (N_A_LAYERS, N_LRU_BLOCKS, LRU_BLOCK, LRU_BLOCK), LRU_BLOCK ** -0.5)
    a_b_i = nrm(ks[15], (N_A_LAYERS, D_RNN), 0.01)
    a_c = jax.random.uniform(ks[16], (N_A_LAYERS, D_RNN), f32, minval=0.9, maxval=0.999)
    a_base = a_c ** (1.0 / LRU_C)
    a_lambda = jnp.log(a_base) - jnp.log1p(-a_base)
    a_w_out = nrm(ks[17], (N_A_LAYERS, D_RNN, D_MODEL), D_RNN ** -0.5)
    kv_norm = 1.0 + nrm(ks[18], (D_MODEL,), 0.05)
    w_k = nrm(ks[19], (D_MODEL, KV_WIDTH), D_MODEL ** -0.5)
    w_v = nrm(ks[20], (D_MODEL, KV_WIDTH), D_MODEL ** -0.5)
    b_w_in = nrm(ks[21], (N_B_LAYERS, D_MODEL, 2 * ATT_WIDTH), D_MODEL ** -0.5)
    b_logit = LOGIT_BIAS_INIT + nrm(ks[23], (N_B_LAYERS, N_HEADS), 0.1)
    b_w_out = nrm(ks[22], (N_B_LAYERS, ATT_WIDTH, D_MODEL), ATT_WIDTH ** -0.5)
    return {"x_prompt": x_prompt, "x_sample": x_sample, "cache_k": cache_k, "cache_v": cache_v,
            "state_conv": state_conv, "state_h": state_h, "page_table": page_table,
            "g_pre": g_pre, "g_post": g_post, "a_w_in": a_w_in, "a_conv_w": a_conv_w,
            "a_conv_b": a_conv_b, "a_w_r": a_w_r, "a_b_r": a_b_r, "a_w_i": a_w_i, "a_b_i": a_b_i,
            "a_lambda": a_lambda, "a_w_out": a_w_out, "kv_norm": kv_norm, "w_k": w_k, "w_v": w_v,
            "b_w_in": b_w_in, "b_logit": b_logit, "b_w_out": b_w_out}

def reference(x_prompt, x_sample, cache_k, cache_v, state_conv, state_h, page_table, g_pre, g_post,
              a_w_in, a_conv_w, a_conv_b, a_w_r, a_b_r, a_w_i, a_b_i, a_lambda, a_w_out, kv_norm,
              w_k, w_v, b_w_in, b_logit, b_w_out):
    weights = (g_pre, g_post, a_w_in, a_conv_w, a_conv_b, a_w_r, a_b_r, a_w_i, a_b_i, a_lambda,
               a_w_out, kv_norm, w_k, w_v, b_w_in, b_logit, b_w_out)
    Bp = x_prompt.shape[0]
    zero_conv = jnp.zeros((Bp, N_A_LAYERS, CONV_W - 1, D_RNN), x_prompt.dtype)
    zero_h = jnp.zeros((Bp, N_A_LAYERS, D_RNN), jnp.float32)
    empty_kv = jnp.zeros((Bp, 0, KV_HEADS, HEAD_DIM), x_prompt.dtype)
    y_prompt, conv_p, h_p, k_p, v_p = run_group(x_prompt, zero_conv, zero_h, empty_kv, empty_kv, *weights)
    Bs, n_pages = page_table.shape
    past_k = cache_k[page_table].reshape(Bs, n_pages * PAGE_SIZE, KV_HEADS, HEAD_DIM)
    past_v = cache_v[page_table].reshape(Bs, n_pages * PAGE_SIZE, KV_HEADS, HEAD_DIM)
    y_sample, conv_s, h_s, k_s, v_s = run_group(x_sample, state_conv, state_h, past_k, past_v, *weights)
    return (y_prompt, y_sample, conv_p, h_p, k_p, v_p, conv_s, h_s, k_s, v_s)


_drawn_inputs = setup_inputs


def setup_inputs(seed=0):
    import zlib

    import numpy as np

    out = dict(_drawn_inputs(seed))
    spreads = {}
    factors = {'a_b_r': 24.453, 'a_b_i': 8.0}
    for name, (base, spread) in spreads.items():
        noise = np.random.default_rng([zlib.crc32(name.encode()), seed]).standard_normal(out[name].shape)
        drawn = base * np.exp(spread * noise) if base else spread * noise
        out[name] = __import__('jax').numpy.asarray(drawn.astype(out[name].dtype))
    for name, factor in factors.items():
        out[name] = (out[name] * factor).astype(out[name].dtype)
    return out
```

```python
from contextlib import ExitStack

import concourse.bass as bass
from concourse import mybir

F32 = mybir.dt.float32
F32R = mybir.dt.float32r
I32 = mybir.dt.int32
ALU = mybir.AluOpType
ACT = mybir.ActivationFunctionType

P = 128
D = 2048
KD = D // P
SEQ = 512
NB, NT = 8, 4
NS = NB * NT
TOK = SEQ + NS
HALF = TOK // 2
RNN = 2560
KR = RNN // P
BLK = 256
NBLK = RNN // BLK
CW = 4
SW = CW - 1
LRU_C = 8.0
DH = 128
NH, NKV, GRP = 16, 4, 4
KVW = NKV * DH
PAGE = 128
NPAGE = 8
EPS = 1e-6
SCALE = DH ** -0.5
UT = 8

ROW_CW, ROW_CB, ROW_BR, ROW_BI, ROW_LAM, ROW_SC, ROW_SH = 0, 4, 5, 6, 7, 8, 8 + NB * SW
CROWS = ROW_SH + NB
ST_CP, ST_HP, ST_CS, ST_HS = 0, SW, SW + 1, SW + 1 + NB * SW
SCOLS = ST_HS + NB
G_PRE0, G_PRE1, G_POST0, G_POST1, G_KV = range(5)
XPW = SW + SEQ + NB * (SW + NT)
XPS = SW + SEQ

A_UNITS = 8 * NBLK
B_TILES = (8, 8, 4)
B0 = A_UNITS
D0 = B0 + 3 * KD
E0 = D0 + 2 * (2 * NKV + 2 * NH)
UNITS = E0 + 2 * KD
SB0 = 4 * NBLK
SD0 = SB0 + KD
SE0 = SD0 + 2 * NKV + 2 * NH
STEPS_A = 2 + 2 + 2 + 2 * 4 + 2 * 3
STEPS_D = 4 * GRP + 1


class Steps:

    def __init__(self, eng, sem):
        self.eng, self.sem, self.origin, self.local = eng, sem, 0, 0

    def done(self, ins):
        ins.then_inc(self.sem, 1)
        self.local += 1
        self.eng.wait_ge(self.sem, self.origin + self.local)

    def loop(self, i, first, per):
        self.start, self.per = self.origin + self.local, per
        self.origin, self.local = (i - first) * per + self.start, 0

    def leave(self, rounds):
        assert self.local == self.per, self.local
        self.origin, self.local = self.start + rounds * self.per, 0


def build(nc, a, out):
    ctx = ExitStack()
    with ctx:
        def sem(name):
            return ctx.enter_context(nc.semaphore(name))

        base = (nc.sbuf_base + 31) // 32 * 32 if isinstance(nc.sbuf_base, int) else 0
        at = [base]

        def sb(name, shape, dt=F32, offset=None):
            size = 4
            for n in shape[1:]:
                size *= n
            if offset is None:
                offset = at[0]
                at[0] += (size + 31) // 32 * 32
            return nc.alloc_sbuf_tensor_at(name, list(shape), dt, offset=offset), offset

        U, U_AT = sb("U", [P, 40, TOK], F32R)
        Y, Y_AT = sb("Y", [P, KR, TOK])
        raw, _ = sb("raw", [P, 2, UT, P])
        WS, _ = sb("WS", [P, 2, 2, UT, P], F32R)
        GW, GW_AT = sb("GW", [P, 2, 2, BLK])
        GWS, GWS_AT = sb("GWS", [P, 2, 2, 2, BLK], F32R)
        T, T_AT = sb("T", [P, 12, 572])
        RS, _ = sb("RS", [P, TOK])
        CH, _ = sb("CH", [P, KR, CROWS])
        C8, _ = sb("C8", [P, 2, KR])
        SM, _ = sb("SM", [P, 8, KR])
        GN, _ = sb("GN", [P, KD, 5])
        SO, _ = sb("SO", [P, KR, SCOLS])
        IDN, _ = sb("IDN", [P, P])
        ONE, _ = sb("ONE", [P, P])
        TRI, _ = sb("TRI", [P, 2, P], F32R)
        MSK, _ = sb("MSK", [P, 2 * P])
        BIAS, _ = sb("BIAS", [P, NH])
        QS, _ = sb("QS", [P, NH * NS])
        KST, _ = sb("KST", [P, NKV, NS])
        VST, _ = sb("VST", [P, KVW])
        PT, _ = sb("PT", [1, NB * NPAGE], I32)
        KVP, _ = sb("KVP", [P, 4, SEQ], F32R, offset=GWS_AT)
        KPG, _ = sb("KPG", [P, 2, NB, KVW], offset=U_AT)
        VPG, _ = sb("VPG", [P, 2, NB, KVW], offset=U_AT + 2 * NB * KVW * 4)
        KPT, _ = sb("KPT", [P, 4, KVW], offset=U_AT + 4 * NB * KVW * 4)
        OA, _ = sb("OA", [NKV * GRP * NT, 6, KVW], offset=U_AT + (4 * NB + 4) * KVW * 4)
        YO, _ = sb("YO", [P, 5, D], offset=U_AT)
        xin, _ = sb("xin", [P, 5, D], offset=Y_AT)
        prow, _ = sb("prow", [CROWS, RNN], offset=GW_AT)
        grow, _ = sb("grow", [5, D], offset=U_AT + 32 * TOK * 4)
        srow, _ = sb("srow", [SCOLS, RNN], offset=GW_AT)

        PS = ctx.enter_context(nc.psum_tensor("PS", [P, 2, 2, 512], F32))
        Z = ctx.enter_context(nc.psum_tensor("Z", [P, 2, 2, 512], F32))

        xT = nc.dram_tensor("scratch_x", (KD, P, TOK), F32, kind="Internal").ap()
        x1T = nc.dram_tensor("scratch_x1", (KD, P, TOK), F32, kind="Internal").ap()

        masks = sem("masks")
        bias_in = sem("bias_in")
        pt_in = sem("pt_in")
        x_back = [sem(f"x_back{n}") for n in range(4)]
        x1_sum = sem("x1_sum")
        x1_high = sem("x1_high")
        x1_low = sem("x1_low")
        x1_kept = sem("x1_kept")
        w_fold = sem("w_fold")
        k_high = sem("k_high")
        k_low = sem("k_low")
        v_high = sem("v_high")
        v_low = sem("v_low")
        kv_t = sem("kv_t")
        kv_t_out = sem("kv_t_out")
        k_stored = sem("k_stored")
        v_stored = sem("v_stored")
        q_high = sem("q_high")
        q_low = sem("q_low")
        sgb_ready = sem("sgb_ready")
        silu_done = sem("silu_done")
        qk_done = sem("qk_done")
        z_out = sem("z_out")
        l_ready = sem("l_ready")
        sp_ready = sem("sp_ready")
        sp_high = sem("sp_high")
        sp_low = sem("sp_low")
        later_done = sem("later_done")
        arg_ready = sem("arg_ready")
        rest_done = sem("rest_done")
        at_exp = sem("at_exp")
        at_masked = sem("at_masked")
        at_high = sem("at_high")
        at_low = sem("at_low")
        pv_done = sem("pv_done")
        o_out = sem("o_out")
        y2_high = sem("y2_high")
        y2_low = sem("y2_low")
        y_sum = sem("y_sum")
        yt_done = sem("yt_done")
        yt_out = sem("yt_out")
        yt_out_s = sem("yt_out_s")
        keys_in = [sem("keys_in0"), sem("keys_in1")]
        values_in = [sem("values_in0"), sem("values_in1")]
        kp_t = sem("kp_t")
        kp_even = sem("kp_even")
        kp_odd = sem("kp_odd")
        kp_used = sem("kp_used")
        d_mask = sem("d_mask")
        d_cleared = sem("d_cleared")
        d_z = sem("d_z")
        d_zout = sem("d_zout")
        d_l = sem("d_l")
        d_sp = sem("d_sp")
        d_high = sem("d_high")
        d_low = sem("d_low")
        d_later = sem("d_later")
        d_arg = sem("d_arg")
        d_rest = sem("d_rest")
        d_exp = sem("d_exp")
        d_at = sem("d_at")
        d_pv_b = sem("d_pv_b")
        d_sum_b = sem("d_sum_b")
        d_turned = sem("d_turned")
        d_out = sem("d_out")
        x_in = [sem(f"x_in{t}") for t in range(5)]
        rows_in = sem("rows_in")
        unit_in = [sem("unit_in0"), sem("unit_in1")]
        w_high = sem("w_high")
        w_low = sem("w_low")
        unit_done = sem("unit_done")
        strip_out = sem("strip_out")
        ident = sem("ident")
        ones = sem("ones")
        rows_t = sem("rows_t")
        rows_c = sem("rows_c")
        lam_abs = sem("lam_abs")
        x_t = sem("x_t")
        x_out = sem("x_out")
        x_high = sem("x_high")
        x_low = sem("x_low")
        x_sq = sem("x_sq")
        sq_sum = sem("sq_sum")
        x_kept = [sem(f"x_kept{n}") for n in range(4)]
        ms_done = sem("ms_done")
        ms_out = sem("ms_out")
        ms_root = sem("ms_root")
        gw_in = sem("gw_in")
        gw_high = sem("gw_high")
        gw_low = sem("gw_low")
        xc_ready = sem("xc_ready")
        xc_high = sem("xc_high")
        xc_low = sem("xc_low")
        gates_done = sem("gates_done")
        gates_out = sem("gates_out")
        sg_ready = sem("sg_ready")
        decay = sem("decay")
        q_ready = sem("q_ready")
        q_root = sem("q_root")
        y_done = sem("y_done")
        y_high = sem("y_high")
        y_low = sem("y_low")
        st_t = sem("st_t")
        st_out = sem("st_out")
        dve_step = sem("dve_step")
        act_step = sem("act_step")
        pool_step = sem("pool_step")
        stored = sem("stored")

        assert at[0] <= nc.sbuf_usable_end
        block = ctx.enter_context(nc.Block())

        QR = NKV * GRP * NT

        def value_sums(b):
            return OA[:, b, :] if b < 6 else T[0:QR, 5 if b == 6 else 8, 0:KVW]

        def d_columns(tile):
            return tile.rearrange("p (k b x) -> p k b x", k=NKV, b=NB)

        def d_weights(rows):
            return T[0:rows, 4, 0:SEQ].rearrange("p (b k x) -> p k b x", k=NKV, b=NB)

        def d_bank(b):
            return PS[:, b % 4 // 2, b % 2, :]

        def halves(ap):
            return ap.rearrange("p (a n) -> p a n", a=2)

        def strip_psum(s):
            return PS[:, s % 2, :, 0:HALF]

        w_in_a = a["a_w_in"].rearrange("l (t p) n -> p (l t) n", p=P)
        w_out_a = a["a_w_out"].rearrange("l (t p) n -> p (l t) n", p=P)
        w_r = a["a_w_r"].rearrange("l g (t p) n -> (l g) p t n", p=P)
        w_i = a["a_w_i"].rearrange("l g (t p) n -> (l g) p t n", p=P)

        def y_slot(kt, part):
            n = 2 * kt + part
            return 36 + n if n < 4 else n - 4

        FIRST_Q = (2 * P, 2 * P, P, 0)

        def y_one(ap):
            return ap.rearrange("p o n -> p (o n)")

        @block.sync
        def _(sp):
            for t in range(4):
                sp.dma_start(xin[:, t, :], a["x_prompt"][0, t * P:(t + 1) * P, :]).then_inc(x_in[t], 16)
            sp.dma_start(xin[0:NS, 4, :], a["x_sample"].rearrange("b t d -> (b t) d")).then_inc(x_in[4], 16)
            sp.dma_start(grow[0:2, :], a["g_pre"]).then_inc(rows_in, 16)
            sp.dma_start(grow[2:4, :], a["g_post"]).then_inc(rows_in, 16)
            sp.dma_start(grow[4:5, :], a["kv_norm"].rearrange("(o n) -> o n", o=1)).then_inc(rows_in, 16)
            sp.dma_start(prow[0:4, :], a["a_conv_w"][0]).then_inc(rows_in, 16)
            for row, name in ((ROW_CB, "a_conv_b"), (ROW_BR, "a_b_r"), (ROW_BI, "a_b_i"), (ROW_LAM, "a_lambda")):
                sp.dma_start(prow[row:row + 1, :], a[name]).then_inc(rows_in, 16)
            sp.dma_start(prow[ROW_SC:ROW_SH, :], a["state_conv"].rearrange("b l w n -> (b l w) n")).then_inc(rows_in, 16)
            sp.dma_start(prow[ROW_SH:CROWS, :], a["state_h"].rearrange("b l n -> (b l) n")).then_inc(rows_in, 16)

            def load_unit(m, slot, src, tiles=UT, reused=True):
                if reused:
                    sp.wait_ge(w_low, m - 1)
                sp.dma_start(raw[:, slot, 0:tiles, :], src).then_inc(unit_in[slot], 16)

            def load_block(i, first):
                for s, col in enumerate((0, P, RNN, RNN + P)):
                    for u in range(2):
                        load_unit(i * 8 + 2 * s + u, u,
                                  w_in_a[:, u * UT:(u + 1) * UT, bass.ds(i * BLK + col, P)],
                                  reused=not first or s > 0)
                    if s == 0:
                        if first:
                            sp.wait_ge(rows_c, 4)
                        else:
                            sp.wait_ge(gw_low, i)
                        sp.dma_start(GW[:, 0, :, :], w_r[bass.ds(i, 1)].rearrange("o p t n -> p (o t) n")).then_inc(gw_in, 16)
                        sp.dma_start(GW[:, 1, :, :], w_i[bass.ds(i, 1)].rearrange("o p t n -> p (o t) n")).then_inc(gw_in, 16)
                    if s == 0 and first:
                        for f in range(KD):
                            sp.wait_ge(x_out, f + 1)
                            sp.dma_start(xT[f], T[:, f % 4, 0:TOK]).then_inc(x_kept[f % 4], 16)

            sp.dma_start(BIAS[:], a["b_logit"].to_broadcast([P, NH])).then_inc(bias_in, 16)
            sp.dma_start(PT[:], a["page_table"].rearrange("b n -> (b n)").rearrange("(o n) -> o n", o=1)).then_inc(pt_in, 16)
            load_block(0, True)
            with sp.Fori(1, NBLK) as i:
                load_block(i, False)

            def load_pair_b(i):
                for s in range(2):
                    t0 = 0
                    for u, tiles in enumerate(B_TILES):
                        n = 3 * s + u
                        load_unit(i * 6 + (B0 + n), n % 2,
                                  w_out_a[:, t0:t0 + tiles, bass.ds(i * 2 * P + s * P, P)], tiles)
                        t0 += tiles

            with sp.Fori(0, KD // 2) as i:
                load_pair_b(i)

            def reload(src, kept, o):
                if kept:
                    sp.wait_ge(x1_kept, 16 * KD)
                else:
                    sp.wait_ge(x_kept[o % 4], 16 * (o // 4 + 1))
                sp.dma_start(T[:, o % 4, 0:TOK], src[o]).then_inc(x_back[o % 4], 16)

            w_kv = (a["w_k"].rearrange("(t p) n -> p t n", p=P), a["w_v"].rearrange("(t p) n -> p t n", p=P))
            w_in_b = a["b_w_in"].rearrange("l (t p) n -> p (l t) n", p=P)
            w_out_b = a["b_w_out"].rearrange("l (t p) n -> p (l t) n", p=P)

            def load_kv(k, strips=(0, 1)):
                for s in strips:
                    for u in range(2):
                        load_unit(k * 20 + (D0 + 2 * s + u), u,
                                  w_kv[s][:, u * UT:(u + 1) * UT, bass.ds(k * DH, DH)])

            def load_qg(k):
                for g in range(GRP):
                    for s in range(2):
                        for u in range(2):
                            load_unit(k * 20 + (D0 + 4 + 4 * g + 2 * s + u), u,
                                      w_in_b[:, u * UT:(u + 1) * UT, bass.ds(k * GRP * DH + (g * DH + s * D), DH)])

            load_kv(0, (0,))
            sp.wait_ge(y_done, KR)
            for o in range(4):
                reload(xT, False, o)
            load_kv(0, (1,))
            for o in range(KD):
                sp.wait_ge(x1_sum, o + 1)
                sp.dma_start(x1T[o], Y[:, o, :]).then_inc(x1_kept, 16)
                if o + 4 < KD:
                    reload(xT, False, o + 4)
            sp.wait_ge(st_out, 5)
            conv_p, h_p, conv_s, h_s = out[2], out[3], out[6], out[7]
            sp.dma_start(conv_p[0, 0], srow[ST_CP:ST_CP + SW, :]).then_inc(stored, 16)
            sp.dma_start(h_p[0], srow[ST_HP:ST_HP + 1, :]).then_inc(stored, 16)
            sp.dma_start(conv_s.rearrange("b l w n -> (b l w) n"), srow[ST_CS:ST_CS + NB * SW, :]).then_inc(stored, 16)
            sp.dma_start(h_s.rearrange("b l n -> (b l) n"), srow[ST_HS:SCOLS, :]).then_inc(stored, 16)
            load_qg(0)
            with sp.Fori(1, NKV) as k:
                load_kv(k)
                load_qg(k)

            def load_pair_e(i, strips=(0, 1)):
                for s in strips:
                    for u in range(2):
                        load_unit(i * 4 + (E0 + 2 * s + u), u,
                                  w_out_b[:, u * UT:(u + 1) * UT, bass.ds(i * 2 * P + s * P, P)])

            load_pair_e(0, (0,))
            sp.wait_ge(pt_in, 16)
            sp.wait_ge(unit_done, E0)

            def load_pages(n, slot, pages, cache, arrived, free=None):
                for b in range(NB):
                    page = sp.value_load(PT[0:1, bass.ds(n * -1 + (b * NPAGE + NPAGE), 1)], min_val=0,
                                         max_val=cache.shape[0] - 1)
                    if b == 0 and free:
                        sp.wait_ge(*free)
                    sp.dma_start(pages[:, slot, b, :], cache[bass.ds(page, 1)].rearrange("o s k d -> s (o k d)"))\
                        .then_inc(arrived[slot], 16)

            def load_step(n, slot, reused):
                load_pages(n, slot, KPG, a["cache_k"], keys_in, (kp_t, n * 8 - 16) if reused else None)
                load_pages(n, slot, VPG, a["cache_v"], values_in, (d_pv_b, n * 8 - 8) if reused else None)

            load_step(1, 1, False)
            load_step(2, 0, False)
            with sp.Fori(1, NPAGE // 2) as i:
                load_step(i * 2 + 1, 1, True)
                load_step(i * 2 + 2, 0, True)
            load_pair_e(0, (1,))
            with sp.Fori(1, KD // 2) as i:
                load_pair_e(i)
            for o in range(KD):
                if o >= 4:
                    sp.wait_ge(y_sum, o - 3)
                else:
                    sp.wait_ge(d_out, 1)
                reload(x1T, True, o)
            y_p, y_s = out[0], out[1].rearrange("b t d -> (b t) d")
            for n in range(4):
                sp.wait_ge(yt_out, 4 * n + 4)
                sp.wait_ge(yt_out_s, 4 * n + 4)
                cols = slice(n * SEQ, (n + 1) * SEQ)
                sp.dma_start(y_p[0].rearrange("(t p) d -> p t d", p=P)[:, :, cols], YO[:, 0:4, cols]).then_inc(stored, 16)
                sp.dma_start(y_s[:, cols], YO[0:NS, 4, cols]).then_inc(stored, 16)
            sp.wait_ge(stored, 64 + 128)
            sp.wait_ge(k_stored, NKV * 32)
            sp.wait_ge(v_stored, NKV * 32)

        @block.gpsimd
        def _(pool):
            steps = Steps(pool, pool_step)
            steps.done(pool.memset(IDN[:], 0.0))
            pool.affine_select(out=IDN[:], in_=IDN[:], compare_op=ALU.not_equal, fill=1.0, base=0,
                               pattern=[[-1, P]], channel_multiplier=1).then_inc(ident, 1)
            pool.memset(ONE[:], 1.0).then_inc(ones, 1)
            tri = T[:, 10, 0:2 * P].rearrange("p (a n) -> p a n", a=2)
            steps.done(pool.memset(tri, 1.0))
            pool.affine_select(out=tri[:, 0], in_=tri[:, 0], compare_op=ALU.is_gt, fill=0.0, base=0,
                               pattern=[[-1, P]], channel_multiplier=1)
            steps.done(pool.affine_select(out=tri[:, 1], in_=tri[:, 1], compare_op=ALU.is_ge, fill=0.0, base=0,
                                          pattern=[[1, P]], channel_multiplier=-1))
            steps.done(pool.tensor_copy(TRI[:], tri))
            steps.done(pool.memset(MSK[:], 1.0))
            steps.done(pool.affine_select(out=MSK[:], in_=MSK[:], compare_op=ALU.is_gt, fill=0.0, base=-P,
                                          pattern=[[1, 2 * P]], channel_multiplier=-1))
            pool.memset(VST[:], 0.0).then_inc(masks, 1)

            def fold(of, m, slot, gain):
                pool.wait_ge(unit_in[slot], of * 8 + 16 * (m // 2 + 1))
                g = GN[:, slot * UT:(slot + 1) * UT, gain:gain + 1].to_broadcast([P, UT, P])
                pool.tensor_tensor(raw[:, slot], raw[:, slot], g, ALU.mult).then_inc(w_fold, 1)

            def add_square(n, par, norm_no, first):
                pool.wait_ge(x_sq, n + 1)
                sq = T[:, 4 + par, 0:TOK]
                if first:
                    if norm_no:
                        pool.wait_ge(ms_done, norm_no)
                    ins = pool.tensor_copy(T[:, 6, 0:TOK], sq)
                else:
                    pool.wait_ge(sq_sum, n)
                    ins = pool.tensor_tensor(T[:, 6, 0:TOK], T[:, 6, 0:TOK], sq, ALU.add)
                ins.then_inc(sq_sum, 1)

            for f in range(KD):
                add_square(f, f % 2, 0, f == 0)
            for n in range(2):
                add_square(KD + n, n, 1, n == 0)
            with pool.Fori(1, KD // 2 - 1) as i:
                for n in range(2):
                    add_square(i * 2 + (KD + n), n, 1, False)
            for n in range(2):
                add_square(2 * KD - 2 + n, n, 1, False)
                fold(0, D0 + n, n, G_KV)
            for o in range(KD):
                add_square(2 * KD + o, o % 2, 2, o == 0)

            k_p, v_p, k_s, v_s = out[4], out[5], out[8], out[9]

            def store_kv(k, which):
                tile, small, sem_, to, to_s = ((T[:, 9, 0:SEQ], T[0:NS, 11, 0:DH], k_stored, k_p, k_s),
                                               (T[:, 10, 0:SEQ], VST[0:NS, bass.ds(k * DH, DH)], v_stored, v_p, v_s))[which]
                pool.dma_start(to[0].rearrange("(t p) k d -> p t k d", p=P)[:, :, bass.ds(k, 1), :]
                               .rearrange("p t o d -> p t (o d)"), tile.rearrange("p (t d) -> p t d", t=4)).then_inc(sem_, 16)
                pool.dma_start(to_s.rearrange("b t k d -> (b t) k d")[:, bass.ds(k, 1), :]
                               .rearrange("p o d -> p (o d)"), small).then_inc(sem_, 16)

            def folds(k, first):
                for n in range(4):
                    if not (first and n < 2):
                        fold(k * 20, D0 + n, n % 2, G_KV)
                for n in range(4, 20):
                    if n == 8:
                        pool.wait_ge(kv_t_out, k * 2 + 2)
                    fold(k * 20, D0 + n, n % 2, G_PRE1)
                    if n == 8:
                        store_kv(k, 0)
                        store_kv(k, 1)

            folds(0, True)
            with pool.Fori(1, NKV) as k:
                folds(k, False)
            pool.wait_ge(silu_done, NH)
            pool.wait_ge(k_stored, NKV * 32)
            m8 = T[0:NS, 7, 0:SEQ].rearrange("p (k b g t) -> p k b g t", k=NKV, b=NB, g=GRP)
            pool.wait_ge(v_low, NKV)
            steps.done(pool.memset(T[0:NS, 7, 0:SEQ], 1.0))
            for k in range(NKV):
                steps.done(pool.affine_select(out=m8[:, k], in_=m8[:, k], compare_op=ALU.is_gt, fill=0.0, base=0,
                                              pattern=[[NT, NB], [0, GRP], [1, NT]], channel_multiplier=-1))
                ins = pool.affine_select(out=m8[:, k], in_=m8[:, k], compare_op=ALU.is_ge, fill=0.0, base=0,
                                         pattern=[[-NT, NB], [0, GRP], [0, NT]], channel_multiplier=1)
            ins.then_inc(d_mask, 1)
            pool.wait_ge(pv_done, NH * 4)
            pool.wait_ge(q_low, NH)
            pool.memset(OA[:], 0.0)
            for b in (6, 7):
                ins = pool.memset(value_sums(b), 0.0)
            ins.then_inc(d_cleared, 1)
            for n in range(2):
                add_square(3 * KD + n, n, 3, n == 0)
            with pool.Fori(1, KD // 2) as i:
                for n in range(2):
                    add_square(i * 2 + (3 * KD + n), n, 3, False)

        @block.tensor
        def _(pe):
            def three_pass(psum, w_hi, w_lo, x_hi, x_lo, first, last):
                pe.matmul(psum, w_hi, x_hi, start=first, stop=False)
                pe.matmul(psum, w_hi, x_lo, start=False, stop=False)
                return pe.matmul(psum, w_lo, x_hi, start=False, stop=last)

            def unit(m, slot, s, tiles, hi_of, lo_of, first, last, wait_tile=None, halfway=None):
                pe.wait_ge(w_low, m + 1)
                for c, kt in enumerate(tiles):
                    if halfway is not None and c == 2:
                        halfway()
                    if wait_tile is not None:
                        wait_tile(kt)
                    for h in range(2):
                        cols = slice(h * HALF, (h + 1) * HALF)
                        ins = three_pass(PS[:, s % 2, h, 0:HALF], WS[:, slot, 0, c, :], WS[:, slot, 1, c, :],
                                         U[:, hi_of(kt), cols], U[:, lo_of(kt), cols],
                                         first and c == 0, last and c == len(tiles) - 1)
                ins.then_inc(unit_done, 1)

            def x_hi(kt):
                return kt

            def x_lo(kt):
                return KD + kt

            pe.wait_ge(ident, 1)
            pe.wait_ge(rows_in, 16 * 10)
            for t in range(KR):
                ins = pe.transpose(PS[:, 0, t // 10, (t % 10) * CROWS:(t % 10 + 1) * CROWS],
                                   prow[:, t * P:(t + 1) * P], IDN[0:CROWS, 0:CROWS])
            ins.then_inc(rows_t, 1)
            for t in range(KD):
                ins = pe.transpose(PS[:, 1, 0, t * 5:(t + 1) * 5], grow[:, t * P:(t + 1) * P], IDN[0:5, 0:5])
            ins.then_inc(rows_t, 1)
            for f in range(KD):
                if f >= 2:
                    pe.wait_ge(x_out, f - 1)
                for t in range(4):
                    if f == 0:
                        pe.wait_ge(x_in[t], 16)
                    pe.transpose(Z[:, f % 2, 0, t * P:(t + 1) * P], xin[:, t, f * P:(f + 1) * P], IDN[:])
                if f == 0:
                    pe.wait_ge(x_in[4], 16)
                pe.transpose(Z[:, f % 2, 1, 0:NS], xin[0:NS, 4, f * P:(f + 1) * P], IDN[0:NS, 0:NS]).then_inc(x_t, 1)

            def norm_sums(k, acc):
                for h in range(2):
                    ins = pe.matmul(Z[:, 0, h, 0:HALF], ONE[:], acc[:, h * HALF:(h + 1) * HALF], start=True, stop=True)
                ins.then_inc(ms_done, 1)

            def block_a(i, first):
                for s in range(4):
                    if not (first and s < 2):
                        pe.wait_ge(strip_out, i * 4 + (s - 1))
                    for u in range(2):
                        def wait_tile(kt):
                            pe.wait_ge(x_low, kt + 1)
                        unit(i * 8 + (2 * s + u), u, s, range(u * UT, (u + 1) * UT), x_hi, x_lo,
                             u == 0, u == 1, wait_tile if first and s == 0 else None)
                    if first and s == 0:
                        pe.wait_ge(ones, 1)
                        pe.wait_ge(sq_sum, KD)
                        norm_sums(0, T[:, 6, 0:TOK])
                pe.wait_ge(gw_low, i + 1)
                pe.wait_ge(xc_low, i * 2 + 2)
                if first:
                    pe.wait_ge(ms_out, 1)
                for o in range(2):
                    for g in range(2):
                        n = 2 * o + g
                        if not (first and n < 2):
                            pe.wait_ge(gates_out, i * 4 + (n - 1))
                        for k in range(2):
                            for h in range(2):
                                cols = slice(h * HALF, (h + 1) * HALF)
                                ins = three_pass(Z[:, g, h, 0:HALF], GWS[:, 0, g, k, o * P:(o + 1) * P],
                                                 GWS[:, 1, g, k, o * P:(o + 1) * P],
                                                 U[:, 32 + 2 * k, cols], U[:, 33 + 2 * k, cols], k == 0, k == 1)
                        ins.then_inc(gates_done, 1)

            block_a(0, True)
            with pe.Fori(1, NBLK) as i:
                block_a(i, False)

            def pair_b(i, first):
                for s in range(2):
                    pe.wait_ge(strip_out, i * 2 + (SB0 + s - 1))
                    t0 = 0
                    for u, tiles in enumerate(B_TILES):
                        def wait_tile(kt):
                            pe.wait_ge(y_low, kt + 1)
                        unit(i * 6 + (B0 + 3 * s + u), (3 * s + u) % 2, s, range(t0, t0 + tiles),
                             lambda kt: y_slot(kt, 0), lambda kt: y_slot(kt, 1), u == 0, u == 2,
                             wait_tile if first and s == 0 else None)
                        t0 += tiles

            pair_b(0, True)
            with pe.Fori(1, KD // 2) as i:
                pair_b(i, False)
            pe.wait_ge(gates_out, 4 * NBLK)
            for n in range(5):
                if n >= 2:
                    pe.wait_ge(st_out, n - 1)
                for t in range(4):
                    ins = pe.transpose(Z[0:SCOLS, 1, n % 2, t * P:(t + 1) * P], SO[:, 4 * n + t, :], IDN[:])
                ins.then_inc(st_t, 1)
            pe.wait_ge(sq_sum, 2 * KD)
            norm_sums(1, T[:, 6, 0:TOK])

            zs, later_sum, o_sum = Z[:, 0], Z[:, 1, 0], Z[:, 1, 1]

            def qk(k, g, s):
                a_ = k * 16 + (4 * g + s)
                q0, j = FIRST_Q[s], 3 - s
                if s == 0:
                    pe.wait_ge(q_low, k * GRP + (g + 1))
                    if g == 0:
                        pe.wait_ge(k_low, k + 1)
                        pe.wait_ge(kv_t_out, k * 2 + 2)
                if g or s > 1:
                    pe.wait_ge(z_out, a_ - 1)
                three_pass(zs[:, s % 2, q0:SEQ], KVP[:, 0, j * P:(j + 1) * P], KVP[:, 1, j * P:(j + 1) * P],
                           U[:, 32 + 2 * (g % 2), q0:SEQ], U[:, 33 + 2 * (g % 2), q0:SEQ], True, True).then_inc(qk_done, 1)

            def later(k, g, s):
                a_ = k * 16 + (4 * g + s)
                q0 = FIRST_Q[s]
                pe.wait_ge(sp_low, a_ + 1)
                if not (isinstance(a_, int) and a_ == 0):
                    pe.wait_ge(arg_ready, a_)
                pe.matmul(later_sum[:, q0:SEQ], TRI[:, 0, :], U[:, 36, q0:SEQ], start=s == 0, stop=False, skip_group_check=True)
                pe.matmul(later_sum[:, q0:SEQ], TRI[:, 0, :], U[:, 37, q0:SEQ], start=False, stop=s == 3,
                          skip_group_check=True).then_inc(later_done, 1)

            def rest(k, g, s):
                q0 = FIRST_Q[s]
                pe.wait_ge(arg_ready, k * 16 + (4 * g + s + 1))
                pe.matmul(later_sum[:, q0:SEQ], TRI[:, 1, :], U[:, 36, q0:SEQ], start=False, stop=False, skip_group_check=True)
                pe.matmul(later_sum[:, q0:SEQ], TRI[:, 1, :], U[:, 37, q0:SEQ], start=False, stop=False,
                          skip_group_check=True).then_inc(rest_done, 1)

            def pv(k, g, s):
                q0, j = FIRST_Q[s], 3 - s
                pe.wait_ge(at_low, k * 16 + (4 * g + s + 1))
                if s == 0:
                    if g == 0:
                        pe.wait_ge(v_low, k + 1)
                    if not (isinstance(k, int) and k == 0 and g == 0):
                        pe.wait_ge(o_out, k * GRP + g)
                o = o_sum[:, q0:SEQ]
                hi, lo = KVP[:, 2, j * P:(j + 1) * P], KVP[:, 3, j * P:(j + 1) * P]
                pe.matmul(o, hi, U[:, 38, q0:SEQ], start=s == 0, stop=False, skip_group_check=True)
                pe.matmul(o, hi, U[:, 39, q0:SEQ], start=False, stop=False, skip_group_check=True)
                pe.matmul(o, lo, U[:, 38, q0:SEQ], start=False, stop=s == 3, skip_group_check=True).then_inc(pv_done, 1)

            def turn_kv(k, which):
                pe.wait_ge(strip_out, k * 10 + (SD0 + which + 1))
                if which == 0:
                    if isinstance(k, int) and k == 0:
                        pe.wait_ge(ms_out, 3)
                    else:
                        pe.wait_ge(z_out, k * 16)
                else:
                    pe.wait_ge(kv_t_out, k * 2 + 1)
                for j in range(4):
                    pe.transpose(zs[:, 0, j * P:(j + 1) * P], T[:, 6 + which, j * P:(j + 1) * P], IDN[:])
                pe.transpose(zs[0:NS, 1, 0:P], T[:, 6 + which, SEQ:TOK], IDN[:]).then_inc(kv_t, 1)

            def pair(k, off, att=None, tail=None, turn=False, units=True, first=False):
                for s in range(4):
                    def between():
                        if s:
                            rest(*att, s - 1)
                        if s < 3:
                            qk(*att, s + 1)
                    if att:
                        if s == 0:
                            qk(*att, 0)
                        if not units:
                            between()
                    if units:
                        if s % 2 == 0:
                            pe.wait_ge(strip_out, k * 10 + (SD0 + off // 2 + s // 2 - 1))
                        def wait_tile(kt):
                            pe.wait_ge(x1_low, kt + 1)
                        unit(k * 20 + (D0 + off + s), s % 2, s // 2, range(s % 2 * UT, (s % 2 + 1) * UT), x_hi, x_lo,
                             s % 2 == 0, s % 2 == 1, wait_tile if first and s < 2 else None,
                             between if att else None)
                        if first and s == 1:
                            pe.wait_ge(sq_sum, 3 * KD)
                            pe.wait_ge(ms_out, 2)
                            norm_sums(2, T[:, 6, 0:TOK])
                    if s == 0 and tail:
                        pv(*tail, 3)
                    if turn and s < 2:
                        turn_kv(k, s)
                    if att:
                        if s:
                            pv(*att, s - 1)
                        later(*att, s)

            pe.wait_ge(masks, 1)
            pair(0, 0, first=True)
            pair(0, 4, turn=True)

            def group(k, whole):
                pair(k, 8, att=(k, 0))
                pair(k, 12, att=(k, 1), tail=(k, 0))
                pair(k, 16, att=(k, 2), tail=(k, 1))
                if whole:
                    pair(k + 1, 0, att=(k, 3), tail=(k, 2))
                    pair(k + 1, 4, tail=(k, 3), turn=True)

            with pe.Fori(0, NKV - 1) as k:
                group(k, True)
            group(NKV - 1, False)
            pair(0, 0, att=(NKV - 1, 3), tail=(NKV - 1, 2), units=False)
            pv(NKV - 1, 3, 3)

            def d_later_keys(n):
                pe.wait_ge(d_low, n + 1)
                if not (isinstance(n, int) and n == 0):
                    pe.wait_ge(d_arg, n)
                    first = False
                else:
                    pe.wait_ge(arg_ready, 64)
                    first = True
                pe.matmul(later_sum, TRI[:, 0, :], KVP[:, 0, :], start=first, stop=False, skip_group_check=True)
                pe.matmul(later_sum, TRI[:, 0, :], KVP[:, 1, :], start=False, stop=False, skip_group_check=True).then_inc(d_later, 1)

            def d_rest_keys(n):
                pe.wait_ge(d_arg, n + 1)
                pe.matmul(later_sum, TRI[:, 1, :], KVP[:, 0, :], start=False, stop=False, skip_group_check=True)
                pe.matmul(later_sum, TRI[:, 1, :], KVP[:, 1, :], start=False, stop=False, skip_group_check=True).then_inc(d_rest, 1)

            def d_values(n, slot, pages=None):
                if isinstance(n, int) and n == 0:
                    pe.wait_ge(d_at, 1)
                else:
                    pe.wait_ge(d_exp, n + 1)
                    pe.wait_ge(values_in[slot], pages)
                for b in range(NB):
                    if b >= 4:
                        pe.wait_ge(d_sum_b, n * 8 + (b - 3))
                    v = VST[:, :] if isinstance(n, int) and n == 0 else VPG[:, slot, b, :]
                    ins = pe.matmul(d_bank(b)[0:QR, :], T[:, 4, b * QR:(b + 1) * QR], v, start=True, stop=True)
                    ins.then_inc(d_pv_b, 1)

            def d_turn(n, slot, b, first):
                if not first and b < 2:
                    pe.wait_ge(d_sum_b, n * 8 - 8)
                if not (first and b < 4):
                    pe.wait_ge(kp_odd if b % 2 else kp_even, n * 4 + (b // 2 - 5))
                for k in range(NKV):
                    ins = pe.transpose(d_bank(b)[:, k * P:(k + 1) * P], KPG[:, slot, b, k * DH:(k + 1) * DH], IDN[:])
                ins.then_inc(kp_t, 1)

            def d_step(n, slot, pages, before=None, first=False):
                pe.wait_ge(keys_in[slot], pages)
                if not first:
                    pe.wait_ge(d_zout, n - 1)
                else:
                    pe.wait_ge(z_out, 64)
                d_turn(n, slot, 0, first)
                d_turn(n, slot, 1, first)
                for b in range(NB):
                    if b + 2 < NB:
                        d_turn(n, slot, b + 2, first)
                    pe.wait_ge(kp_odd if b % 2 else kp_even, n * 4 + (b // 2 - 3))
                    for k in range(NKV):
                        cols = slice(k * P + b * 16, k * P + b * 16 + 16)
                        ins = pe.matmul(zs[:, slot, cols], KPT[:, b % 4, k * DH:(k + 1) * DH], QS[:, cols], start=True, stop=True)
                    ins.then_inc(kp_used, 1)
                d_values(n - 1, 1 - slot, before)
                d_rest_keys(n - 1)
                d_later_keys(n)

            pe.wait_ge(strip_out, SE0)
            for k in range(NKV):
                ins = pe.matmul(zs[0:NS, 0, k * P:(k + 1) * P], KST[:, k, :], QS[:, k * P:(k + 1) * P], start=True, stop=True)
            ins.then_inc(d_z, 1)
            d_later_keys(0)
            PAGES = 16 * NB
            d_step(1, 1, PAGES, first=True)
            with pe.Fori(1, NPAGE // 2) as i:
                d_step(i * 2, 0, i * PAGES, i * PAGES)
                d_step(i * 2 + 1, 1, i * PAGES + PAGES, i * PAGES)
            d_step(NPAGE, 0, NPAGE // 2 * PAGES, NPAGE // 2 * PAGES)
            d_values(NPAGE, 0, NPAGE // 2 * PAGES)
            pe.wait_ge(d_sum_b, (NPAGE + 1) * NB)
            for b in range(NB):
                for k in range(NKV):
                    ins = pe.transpose(d_bank(k)[:, b * QR:(b + 1) * QR], value_sums(b)[:, k * DH:(k + 1) * DH], IDN[0:QR, 0:QR])
            ins.then_inc(d_turned, 1)

            def pair_e(i, first):
                for s in range(4):
                    if s % 2 == 0:
                        pe.wait_ge(strip_out, i * 2 + (SE0 + s // 2 - 1))
                    def wait_tile(kt):
                        pe.wait_ge(y2_low, kt + 1)
                    unit(i * 4 + (E0 + s), s % 2, s // 2, range(s % 2 * UT, (s % 2 + 1) * UT), x_hi, x_lo,
                         s % 2 == 0, s % 2 == 1, wait_tile if first and s < 2 else None)

            pair_e(0, True)
            with pe.Fori(1, KD // 2) as i:
                pair_e(i, False)
            pe.wait_ge(sq_sum, 4 * KD)
            norm_sums(3, T[:, 6, 0:TOK])
            pe.wait_ge(ms_out, 4)
            for o in range(KD):
                pe.wait_ge(y_sum, o + 1)
                if o >= 2:
                    pe.wait_ge(yt_out, o - 1)
                    pe.wait_ge(yt_out_s, o - 1)
                for t in range(4):
                    pe.transpose(Z[:, o % 2, 0, t * P:(t + 1) * P], Y[:, o, t * P:(t + 1) * P], IDN[:])
                pe.transpose(Z[0:NS, o % 2, 1, 0:P], Y[:, o, SEQ:TOK], IDN[:]).then_inc(yt_done, 1)

        @block.scalar
        def _(act):
            def high(m, slot, n, tiles=UT, before=True, folded=False):
                if before:
                    act.wait_ge(unit_done, m - 1)
                if folded:
                    act.wait_ge(w_fold, m + (1 - D0))
                else:
                    act.wait_ge(unit_in[slot], n * 16 + 16)
                nc.scalar.activation(WS[:, slot, 0, 0:tiles, :], raw[:, slot, 0:tiles, :], ACT.Copy).then_inc(w_high, 1)

            def root(k):
                act.wait_ge(ms_out, k + 1)
                nc.scalar.activation(T[:, 8, 0:TOK], T[:, 7, 0:TOK], ACT.Sqrt).then_inc(ms_root, 1)

            steps = Steps(act, act_step)
            act.wait_ge(rows_c, 1)
            steps.done(nc.scalar.activation(SM[:, 0, :], CH[:, :, ROW_LAM], ACT.Abs))
            nc.scalar.activation(SM[:, 1, :], SM[:, 0, :], ACT.Exp, scale=-1.0).then_inc(lam_abs, 1)
            high(0, 0, 0, before=False)
            high(1, 1, 0, before=False)
            act.wait_ge(rows_c, 2)
            for f in range(KD):
                act.wait_ge(x_out, f + 1)
                nc.scalar.activation(U[:, f, :], T[:, f % 4, 0:TOK], ACT.Copy,
                                     scale=GN[:, f, G_PRE0:G_PRE0 + 1]).then_inc(x_high, 1)
                if f >= 2:
                    act.wait_ge(sq_sum, f - 1)
                nc.scalar.activation(T[:, 4 + f % 2, 0:TOK], T[:, f % 4, 0:TOK], ACT.Square).then_inc(x_sq, 1)
            high(2, 0, 1)
            root(0)

            def chain_decay(i):
                act.wait_ge(gates_out, i * 4 + 4)
                if not (isinstance(i, int) and i == 0):
                    act.wait_ge(y_done, i * 2)
                for j in range(2):
                    nc.scalar.activation(T[:, 8 + j, 0:TOK], T[:, 4 + j, 0:TOK], ACT.Tanh,
                                         scale=C8[:, 1, bass.ds(i * 2 + j, 1)]).then_inc(decay, 1)
                for j in range(2):
                    nc.scalar.activation(T[:, 4 + j, 0:TOK], T[:, 4 + j, 0:TOK], ACT.Exp,
                                         scale=C8[:, 0, bass.ds(i * 2 + j, 1)]).then_inc(decay, 1)

            def chain_root(i):
                for j in range(2):
                    act.wait_ge(q_ready, i * 2 + (j + 1))
                    nc.scalar.activation(T[:, 10 + j, 0:TOK], T[:, 10 + j, 0:TOK], ACT.Sqrt).then_inc(q_root, 1)

            def sigmoid_gate(i, j):
                act.wait_ge(strip_out, i * 4 + (3 + j))
                nc.scalar.activation(T[:, j, SW:SW + TOK], Y[:, bass.ds(i * 2 + j, 1), :].rearrange("p o n -> p (o n)"),
                                     ACT.Sigmoid).then_inc(sg_ready, 1)

            def block_a(i, first):
                for s in range(8):
                    if not (first and s < 2):
                        high(i * 8 + (s + 1), (s + 1) % 2, i * 4 + (s + 1) // 2)
                    if s == 0 and not first:
                        chain_decay(i - 1)
                    if s == 1:
                        act.wait_ge(gw_in, i * 32 + 32)
                        if not first:
                            act.wait_ge(gates_done, i * 4)
                        nc.scalar.activation(GWS[:, 0], GW[:], ACT.Copy).then_inc(gw_high, 1)
                    if s == 2 and not first:
                        chain_root(i - 1)
                    if s in (3, 5):
                        j = (s - 3) // 2
                        act.wait_ge(xc_ready, i * 2 + (j + 1))
                        nc.scalar.activation(U[:, 32 + 2 * j, :], T[:, 2 + j, 0:TOK], ACT.Copy).then_inc(xc_high, 1)
                    if s == 7:
                        sigmoid_gate(i, 0)
                sigmoid_gate(i, 1)
                if not first:
                    act.wait_ge(y_done, i * 2)
                for o in range(2):
                    for g in range(2):
                        act.wait_ge(gates_done, i * 4 + (2 * o + g + 1))
                        nc.scalar.activation(
                            T[:, 4 + 2 * g + o, 0:TOK].rearrange("p (a n) -> p a n", a=2), Z[:, g, :, 0:HALF],
                            ACT.Sigmoid, bias=CH[:, bass.ds(i * 2 + o, 1), ROW_BR + g].rearrange("p o -> p o")).then_inc(gates_out, 1)

            block_a(0, True)
            with act.Fori(1, NBLK) as i:
                block_a(i, False)

            def y_split(kt):
                act.wait_ge(y_done, kt + 1)
                if kt == 2:
                    act.wait_ge(unit_done, A_UNITS)
                nc.scalar.activation(U[:, y_slot(kt, 0), :], Y[:, kt, :], ACT.Copy).then_inc(y_high, 1)

            chain_decay(NBLK - 1)
            for kt in range(8):
                y_split(kt)
            high(B0 + 1, 1, (B0 + 1) // 2)
            chain_root(NBLK - 1)
            for kt in range(8, KR):
                y_split(kt)

            def square(n, par, src):
                act.wait_ge(sq_sum, n - 1)
                nc.scalar.activation(T[:, 4 + par, 0:TOK], src, ACT.Square).then_inc(x_sq, 1)

            def pair_b(i, first, last):
                for n in range(6):
                    if not (first and n == 0):
                        high(i * 6 + (B0 + n + 1), (n + 1) % 2, i * 3 + (B0 + n + 1) // 2, B_TILES[(n + 1) % 3],
                             folded=last and n == 5)
                    if n == 4:
                        act.wait_ge(strip_out, i * 2 + (SB0 + 1))
                        square(i * 2 + KD, 0, y_one(Y[:, bass.ds(i * 2, 1), :]))
                act.wait_ge(strip_out, i * 2 + (SB0 + 2))
                square(i * 2 + (KD + 1), 1, y_one(Y[:, bass.ds(i * 2 + 1, 1), :]))

            pair_b(0, True, False)
            with act.Fori(1, KD // 2 - 1) as i:
                pair_b(i, False, False)
            pair_b(KD // 2 - 1, False, True)
            root(1)
            high(D0 + 1, 1, (D0 + 1) // 2, folded=True)
            for o in range(KD):
                act.wait_ge(x1_sum, o + 1)
                nc.scalar.activation(U[:, o, :], Y[:, o, :], ACT.Copy).then_inc(x1_high, 1)
                square(2 * KD + o, o % 2, Y[:, o, :])
            high(D0 + 2, 0, 0, folded=True)
            root(2)

            def exp_logits(k, g, s):
                a_ = k * 16 + (4 * g + s)
                q = slice(FIRST_Q[s], SEQ)
                act.wait_ge(z_out, a_ + 1)
                if not (isinstance(a_, int) and a_ == 0):
                    act.wait_ge(sp_ready, a_)
                steps.done(nc.scalar.activation(T[:, 1, q], T[:, 0, q], ACT.Abs))
                steps.done(nc.scalar.activation(T[:, 1, q], T[:, 1, q], ACT.Exp, scale=-1.0))
                nc.scalar.activation(T[:, 1, q], T[:, 1, q], ACT.Ln, bias=1.0).then_inc(l_ready, 1)

            def exp_arg(k, g, s):
                a_ = k * 16 + (4 * g + s)
                q = slice(FIRST_Q[s], SEQ)
                act.wait_ge(arg_ready, a_ + 1)
                if not (isinstance(a_, int) and a_ == 0):
                    act.wait_ge(at_low, a_)
                nc.scalar.activation(T[:, 4, q], T[:, 3, q], ACT.Exp).then_inc(at_exp, 1)

            def at_split(k, g, s):
                a_ = k * 16 + (4 * g + s)
                q = slice(FIRST_Q[s], SEQ)
                act.wait_ge(at_masked, a_ + 1)
                if not (isinstance(a_, int) and a_ == 0):
                    act.wait_ge(pv_done, a_)
                nc.scalar.activation(U[:, 38, q], T[:, 4, q], ACT.Copy).then_inc(at_high, 1)

            def sp_split(k, g, s):
                a_ = k * 16 + (4 * g + s)
                q = slice(FIRST_Q[s], SEQ)
                act.wait_ge(sp_ready, a_ + 1)
                if s:
                    act.wait_ge(rest_done, k * 12 + (3 * g + s))
                elif not (isinstance(k, int) and k == 0 and g == 0):
                    act.wait_ge(later_done, a_)
                nc.scalar.activation(U[:, 36, q], T[:, 2, q], ACT.Copy).then_inc(sp_high, 1)

            def turned(k, which):
                act.wait_ge(kv_t, k * 2 + (which + 1))
                if not (isinstance(k, int) and k == 0):
                    act.wait_ge(v_stored if which else k_stored, k * 32)
                nc.scalar.activation(T[:, 9 + which, 0:SEQ], Z[:, 0, 0, :], ACT.Copy)
                small = VST[0:NS, bass.ds(k * DH, DH)] if which else T[0:NS, 11, 0:DH]
                nc.scalar.activation(small, Z[0:NS, 0, 1, 0:P], ACT.Copy).then_inc(kv_t_out, 1)

            def pair(k, off, g=None, att=None, tail=None, gate=None, turn=False, units=True, first=False, last=False):
                for s in range(4):
                    if units and not (first and s < 2):
                        if last and s == 3:
                            high(E0, 0, E0 // 2)
                        else:
                            high(k * 20 + (D0 + off + s + 1), (s + 1) % 2, 0, folded=True)
                    if s == 0 and gate:
                        act.wait_ge(strip_out, gate[0] * 10 + (SD0 + 4 + 2 * gate[1]))
                        if not (isinstance(gate[0], int) and gate[0] == 0 and gate[1] == 0):
                            act.wait_ge(silu_done, gate[0] * GRP + gate[1])
                        nc.scalar.activation(T[:, 8, 0:TOK], y_one(Y[:, bass.ds(gate[0] * GRP + gate[1], 1), :]),
                                             ACT.Sigmoid).then_inc(sgb_ready, 1)
                    if s == 0 and (att or tail):
                        act.preload_act_table_set("natural_log_exp_and_others")
                    before = (*att, s - 1) if att and s else (*tail, 3) if tail and s == 0 else None
                    if before:
                        exp_arg(*before)
                    if att and s == 0:
                        exp_logits(*att, 0)
                    if before:
                        at_split(*before)
                    if att:
                        sp_split(*att, s)
                        if s < 3:
                            exp_logits(*att, s + 1)
                    if turn and s in (1, 2):
                        turned(k, s - 1)
                        if s == 2:
                            act.wait_ge(kv_t_out, k * 2 + 2)
                            if not (isinstance(k, int) and k == 0):
                                act.wait_ge(pv_done, k * 16)
                            nc.scalar.activation(KVP[:, 2, :], T[:, 10, 0:SEQ], ACT.Copy).then_inc(v_high, 1)
                    if s == 3 and g is not None:
                        act.wait_ge(strip_out, k * 10 + (SD0 + 3 + 2 * g))
                        if not (isinstance(k, int) and k == 0 and g < 2):
                            act.wait_ge(qk_done, k * 16 + 4 * (g - 1))
                        nc.scalar.activation(U[:, 32 + 2 * (g % 2), 0:SEQ], T[:, 5, 0:SEQ], ACT.Copy).then_inc(q_high, 1)
                if units and g is None:
                    act.wait_ge(strip_out, k * 10 + (SD0 + 1))
                    if first:
                        act.wait_ge(stored, 64)
                    else:
                        act.wait_ge(qk_done, k * 16)
                    nc.scalar.activation(KVP[:, 0, :], T[:, 6, 0:SEQ], ACT.Copy).then_inc(k_high, 1)

            pair(0, 0, first=True)
            pair(0, 4, g=0, turn=True)

            def group(k, whole):
                pair(k, 8, g=1, att=(k, 0), gate=(k, 0))
                pair(k, 12, g=2, att=(k, 1), tail=(k, 0), gate=(k, 1))
                pair(k, 16, g=3, att=(k, 2), tail=(k, 1), gate=(k, 2), last=not whole)
                if whole:
                    pair(k + 1, 0, att=(k, 3), tail=(k, 2), gate=(k, 3))
                    pair(k + 1, 4, g=0, tail=(k, 3), turn=True)

            with act.Fori(0, NKV - 1) as k:
                steps.loop(k, 0, 32)
                group(k, True)
            steps.leave(NKV - 1)
            group(NKV - 1, False)
            pair(0, 0, att=(NKV - 1, 3), tail=(NKV - 1, 2), gate=(NKV - 1, 3), units=False)
            exp_arg(NKV - 1, 3, 3)
            at_split(NKV - 1, 3, 3)

            high(E0 + 1, 1, (E0 + 1) // 2)

            def d_exps(n, rows):
                q = slice(0, SEQ)
                act.wait_ge(d_zout, n + 1)
                if not (isinstance(n, int) and n == 0):
                    act.wait_ge(d_sp, n)
                steps.done(nc.scalar.activation(T[0:rows, 1, q], T[0:rows, 0, q], ACT.Abs))
                steps.done(nc.scalar.activation(T[0:rows, 1, q], T[0:rows, 1, q], ACT.Exp, scale=-1.0))
                nc.scalar.activation(T[0:rows, 1, q], T[0:rows, 1, q], ACT.Ln, bias=1.0).then_inc(d_l, 1)
                act.wait_ge(d_sp, n + 1)
                if isinstance(n, int) and n == 0:
                    act.wait_ge(pv_done, 64)
                else:
                    act.wait_ge(d_rest, n)
                nc.scalar.activation(KVP[:, 0, :], T[:, 2, q], ACT.Copy).then_inc(d_high, 1)
                act.wait_ge(d_arg, n + 1)
                if not (isinstance(n, int) and n == 0):
                    act.wait_ge(d_pv_b, n * 8)
                nc.scalar.activation(d_weights(rows), d_columns(T[0:rows, 3, q]), ACT.Exp).then_inc(d_exp, 1)

            d_exps(0, NS)
            with act.Fori(1, NPAGE + 1) as n:
                steps.loop(n, 1, 2)
                for b in range(0, NB, 2):
                    act.wait_ge(kp_t, n * 8 + (b - 7))
                    if b >= 4:
                        act.wait_ge(kp_used, n * 8 + (b - 11))
                    nc.scalar.activation(KPT[:, b % 4, :], d_bank(b), ACT.Copy).then_inc(kp_even, 1)
                d_exps(n, P)
            steps.leave(NPAGE)

            act.wait_ge(d_out, 1)
            for o in range(KD):
                nc.scalar.activation(U[:, o, :], Y[:, o, :], ACT.Copy).then_inc(y2_high, 1)

            def pair_e(i, first, last):
                for s in range(4):
                    if not (first and s == 0) and not (last and s == 3):
                        high(i * 4 + (E0 + s + 1), (s + 1) % 2, i * 2 + (E0 + s + 1) // 2)
                    if s == 3:
                        act.wait_ge(strip_out, i * 2 + (SE0 + 1))
                        square(i * 2 + 3 * KD, 0, y_one(Y[:, bass.ds(i * 2, 1), :]))
                act.wait_ge(strip_out, i * 2 + (SE0 + 2))
                square(i * 2 + (3 * KD + 1), 1, y_one(Y[:, bass.ds(i * 2 + 1, 1), :]))

            pair_e(0, True, False)
            with act.Fori(1, KD // 2 - 1) as i:
                pair_e(i, False, False)
            pair_e(KD // 2 - 1, False, True)
            root(3)
            for o in range(KD):
                act.wait_ge(yt_done, o + 1)
                nc.scalar.activation(YO[:, 0:4, o * P:(o + 1) * P], Z[:, o % 2, 0, :].rearrange("p (t n) -> p t n", t=4),
                                     ACT.Copy).then_inc(yt_out, 1)

        @block.vector
        def _(dve):
            steps = Steps(dve, dve_step)
            V = nc.vector

            def low(m, slot, tiles=UT):
                dve.wait_ge(w_high, m + 1)
                V.tensor_tensor(WS[:, slot, 1, 0:tiles, :], raw[:, slot, 0:tiles, :],
                                WS[:, slot, 0, 0:tiles, :].bitcast(F32), ALU.subtract).then_inc(w_low, 1)

            dve.wait_ge(rows_t, 1)
            for n in range(2):
                V.tensor_copy(CH[:, 10 * n:10 * n + 10, :], PS[:, 0, n, 0:10 * CROWS]
                              .rearrange("p (t c) -> p t c", c=CROWS)).then_inc(rows_c if n else dve_step, 1)
                if not n:
                    steps.local += 1
            dve.wait_ge(rows_t, 2)
            V.tensor_copy(GN[:], PS[:, 1, 0, 0:5 * KD].rearrange("p (t c) -> p t c", c=5)).then_inc(rows_c, 1)
            V.memset(T[:, 0:1, 0:1], 0.0).then_inc(rows_c, 1)
            V.memset(T[:, 1:2, 0:1], 0.0).then_inc(rows_c, 1)
            low(0, 0)
            low(1, 1)
            dve.wait_ge(rows_c, 4)
            def x_rest(f):
                dve.wait_ge(x_high, f + 1)
                dve.wait_ge(x_out, f + 1)
                V.scalar_tensor_tensor(U[:, KD + f, :], T[:, f % 4, 0:TOK], GN[:, f, G_PRE0:G_PRE0 + 1],
                                       U[:, f, :].bitcast(F32), ALU.mult, ALU.subtract).then_inc(x_low, 1)

            for f in range(KD):
                xt = T[:, f % 4, 0:TOK]
                dve.wait_ge(x_t, f + 1)
                if f >= 4:
                    dve.wait_ge(x_kept[f % 4], 16 * (f // 4))
                    dve.wait_ge(x_sq, f - 3)
                steps.done(V.tensor_copy(xt[:, 0:SEQ], Z[:, f % 2, 0, :]))
                V.tensor_copy(xt[:, SEQ:TOK], Z[:, f % 2, 1, 0:NS]).then_inc(x_out, 1)
                if f:
                    x_rest(f - 1)
            x_rest(KD - 1)
            dve.wait_ge(lam_abs, 1)
            e, s_, s2, q = (SM[:, n, :] for n in (1, 2, 3, 4))
            steps.done(V.tensor_scalar(s_, e, 2.0, None, ALU.add))
            steps.done(V.reciprocal(s2, s_))
            steps.done(V.tensor_tensor(s_, s2, e, ALU.mult))
            steps.done(V.tensor_tensor(s2, s_, s_, ALU.mult))
            steps.done(V.tensor_scalar(q, s2, 1.0 / 19, None, ALU.mult))
            for n in (17, 15, 13, 11, 9, 7, 5, 3):
                steps.done(V.scalar_tensor_tensor(q, q, 1.0 / n, s2, ALU.add, ALU.mult))
            steps.done(V.scalar_tensor_tensor(q, q, 1.0, s_, ALU.add, ALU.mult))
            steps.done(V.tensor_scalar(s2, CH[:, :, ROW_LAM], -1.0, 0.0, ALU.mult, ALU.max))
            steps.done(V.scalar_tensor_tensor(s_, q, 2.0, s2, ALU.mult, ALU.add))
            steps.done(V.tensor_scalar(C8[:, 0, :], s_, -LRU_C, None, ALU.mult))
            steps.done(V.tensor_scalar(C8[:, 1, :], s_, LRU_C, None, ALU.mult))

            def norm(k):
                ms, y, t = T[:, 7, 0:TOK], T[:, 8, 0:TOK], T[:, 9, 0:TOK]
                dve.wait_ge(ms_done, k + 1)
                V.tensor_scalar(halves(ms), Z[:, 0, :, 0:HALF], 1.0 / D, EPS, ALU.mult, ALU.add).then_inc(ms_out, 1)
                dve.wait_ge(ms_root, k + 1)
                steps.done(V.reciprocal(RS[:], y))
                steps.done(V.tensor_tensor(t, RS[:], RS[:], ALU.mult))
                steps.done(V.tensor_tensor(t, t, ms, ALU.mult))
                steps.done(V.tensor_scalar(t, t, -0.5, 1.5, ALU.mult, ALU.add))
                steps.done(V.tensor_tensor(RS[:], RS[:], t, ALU.mult))

            low(2, 0)
            norm(0)
            for n in range(4):
                dve.wait_ge(x_kept[n], 16 * (KD // 4))
            steps.done(V.memset(T[:, 0:2, 0:SW], 0.0))

            def y_tile(i, j):
                return Y[:, bass.ds(i * 2 + j, 1), :].rearrange("p o n -> p (o n)")

            def param(i, j, row):
                return CH[:, bass.ds(i * 2 + j, 1), row]

            def branch(i, j):
                xp, xc = T[:, j, :], T[:, 2 + j, 0:TOK]
                ps = PS[:, j % 2]
                dve.wait_ge(unit_done, i * 8 + 2 * (j + 1))
                V.tensor_tensor(xp[:, SW:SW + HALF], ps[:, 0, 0:HALF], RS[:, 0:HALF], ALU.mult)
                V.tensor_tensor(xp[:, SW + HALF:XPS], ps[:, 1, 0:SEQ - HALF], RS[:, HALF:SEQ], ALU.mult)
                smp = xp[:, XPS:XPW].rearrange("p (b w) -> p b w", w=SW + NT)
                V.tensor_copy(smp[:, :, 0:SW], CH[:, bass.ds(i * 2 + j, 1), ROW_SC:ROW_SH]
                              .rearrange("p o (b w) -> p (o b) w", w=SW))
                ins = V.tensor_tensor(smp[:, :, SW:SW + NT],
                                      ps[:, 1, SEQ - HALF:HALF].rearrange("p (b t) -> p b t", t=NT),
                                      RS[:, SEQ:TOK].rearrange("p (b t) -> p b t", t=NT), ALU.mult)
                ins.then_inc(strip_out, 1)
                dve.wait_ge(strip_out, i * 4 + (j + 1))
                xcs = xc[:, SEQ:TOK].rearrange("p (b t) -> p b t", t=NT)
                V.tensor_scalar(xc[:, 0:SEQ], xp[:, 0:SEQ], param(i, j, 0), param(i, j, ROW_CB), ALU.mult, ALU.add)
                steps.done(V.tensor_scalar(xcs, smp[:, :, 0:NT], param(i, j, 0), param(i, j, ROW_CB), ALU.mult, ALU.add))
                for k in range(1, CW):
                    V.scalar_tensor_tensor(xc[:, 0:SEQ], xp[:, k:k + SEQ], param(i, j, k), xc[:, 0:SEQ], ALU.mult, ALU.add)
                    ins = V.scalar_tensor_tensor(xcs, smp[:, :, k:k + NT], param(i, j, k), xcs, ALU.mult, ALU.add)
                    if k < CW - 1:
                        steps.done(ins)
                ins.then_inc(xc_ready, 1)
                st = SO[:, bass.ds(i * 2 + j, 1), :].rearrange("p o c -> p (o c)")
                V.tensor_copy(st[:, ST_CP:ST_CP + SW], xp[:, XPS - SW:XPS])
                steps.done(V.tensor_copy(st[:, ST_CS:ST_CS + NB * SW].rearrange("p (b w) -> p b w", w=SW),
                                         smp[:, :, NT:NT + SW]))

            def out_gate(i, j):
                dve.wait_ge(unit_done, i * 8 + (4 + 2 * (j + 1)))
                V.tensor_tensor(halves(y_tile(i, j)), PS[:, j % 2, :, 0:HALF], halves(RS[:]), ALU.mult).then_inc(strip_out, 1)

            def silu(i, j):
                dve.wait_ge(sg_ready, i * 2 + (j + 1))
                steps.done(V.tensor_tensor(y_tile(i, j), y_tile(i, j), T[:, j, SW:SW + TOK], ALU.mult))

            def gated_input(i):
                dve.wait_ge(gates_out, i * 4 + 4)
                for j in range(2):
                    steps.done(V.tensor_tensor(T[:, 6 + j, 0:TOK], T[:, 6 + j, 0:TOK], T[:, 2 + j, 0:TOK], ALU.mult))

            def one_minus_a2(i):
                dve.wait_ge(decay, i * 4 + 4)
                for j in range(2):
                    q = T[:, 10 + j, 0:TOK]
                    av = T[:, 4 + j, 0:TOK]
                    steps.done(V.tensor_tensor(q, av, av, ALU.mult))
                    V.scalar_tensor_tensor(q, q, 1.0, T[:, 8 + j, 0:TOK], ALU.add, ALU.mult).then_inc(q_ready, 1)

            def recur(i, j):
                av, b, h = T[:, 4 + j, 0:TOK], T[:, 10 + j, 0:TOK], T[:, 8 + j, 0:TOK]
                dve.wait_ge(q_root, i * 2 + (j + 1))
                V.tensor_tensor(b, b, T[:, 6 + j, 0:TOK], ALU.mult)
                a0 = av[:, SEQ:TOK].rearrange("p (b t) -> p b t", t=NT)[:, :, 0]
                b0 = b[:, SEQ:TOK].rearrange("p (b t) -> p b t", t=NT)[:, :, 0]
                steps.done(V.tensor_tensor(SM[:, 5, 0:NB], a0, CH[:, bass.ds(i * 2 + j, 1), ROW_SH:CROWS]
                                           .rearrange("p o b -> p (o b)"), ALU.mult))
                V.memset(a0, 0.0)
                steps.done(V.tensor_tensor(b0, b0, SM[:, 5, 0:NB], ALU.add))
                steps.done(V.tensor_tensor_scan(h, av, b, 0.0, ALU.mult, ALU.add))
                st = SO[:, bass.ds(i * 2 + j, 1), :].rearrange("p o c -> p (o c)")
                V.tensor_copy(st[:, ST_HP:ST_HP + 1], h[:, SEQ - 1:SEQ])
                V.tensor_copy(st[:, ST_HS:SCOLS], h[:, SEQ:TOK].rearrange("p (b t) -> p b t", t=NT)[:, :, NT - 1])
                V.tensor_tensor(y_tile(i, j), y_tile(i, j), h, ALU.mult).then_inc(y_done, 1)

            def block_a(i, first):
                for s in range(8):
                    if not (first and s < 2):
                        low(i * 8 + (s + 1), (s + 1) % 2)
                    if s == 0 and not first:
                        silu(i - 1, 1)
                        gated_input(i - 1)
                    if s == 1:
                        dve.wait_ge(gw_high, i + 1)
                        V.tensor_tensor(GWS[:, 1], GW[:], GWS[:, 0].bitcast(F32), ALU.subtract).then_inc(gw_low, 1)
                        if not first:
                            one_minus_a2(i - 1)
                    if s in (2, 4):
                        branch(i, (s - 2) // 2)
                    if s == 3 and not first:
                        recur(i - 1, 0)
                    if s == 5:
                        for j in range(2):
                            dve.wait_ge(xc_high, i * 2 + (j + 1))
                            V.tensor_tensor(U[:, 33 + 2 * j, :], T[:, 2 + j, 0:TOK], U[:, 32 + 2 * j, :].bitcast(F32),
                                            ALU.subtract).then_inc(xc_low, 1)
                        if not first:
                            recur(i - 1, 1)
                    if s == 6:
                        out_gate(i, 0)
                    if s == 7:
                        silu(i, 0)
                out_gate(i, 1)

            block_a(0, True)
            with dve.Fori(1, NBLK) as i:
                steps.loop(i, 1, STEPS_A)
                block_a(i, False)
            steps.leave(NBLK - 1)

            def y_rest(kt):
                dve.wait_ge(y_high, kt + 1)
                V.tensor_tensor(U[:, y_slot(kt, 1), :], Y[:, kt, :], U[:, y_slot(kt, 0), :].bitcast(F32),
                                ALU.subtract).then_inc(y_low, 1)

            last = NBLK - 1
            silu(last, 1)
            gated_input(last)
            one_minus_a2(last)
            for kt in range(8):
                y_rest(kt)
            low(B0 + 1, 1)
            recur(last, 0)
            recur(last, 1)
            for kt in range(8, KR):
                y_rest(kt)

            def out_tile(of, m, n, par):
                dve.wait_ge(unit_done, m)
                V.tensor_copy(halves(y_one(Y[:, bass.ds(of + n, 1), :])), PS[:, par, :, 0:HALF]).then_inc(strip_out, 1)

            def pair_b(i, first):
                for n in range(6):
                    if not (first and n == 0):
                        low(i * 6 + (B0 + n + 1), (n + 1) % 2, B_TILES[(n + 1) % 3])
                    if n == 3:
                        out_tile(i * 2, i * 6 + (B0 + 3), 0, 0)
                out_tile(i * 2, i * 6 + (B0 + 6), 1, 1)

            pair_b(0, True)
            with dve.Fori(1, KD // 2) as i:
                pair_b(i, False)
            for n in range(5):
                dve.wait_ge(st_t, n + 1)
                V.tensor_copy(srow[:, 4 * n * P:4 * (n + 1) * P], Z[0:SCOLS, 1, n % 2, :]).then_inc(st_out, 1)
            norm(1)
            low(D0 + 1, 1)

            def residual(o, gain, done):
                steps.done(V.scalar_tensor_tensor(Y[:, o, :], Y[:, o, :], GN[:, o, gain:gain + 1], RS[:], ALU.mult, ALU.mult))
                turn = o // 4 + (1 if done is x1_sum else 5)
                dve.wait_ge(x_back[o % 4], 16 * turn)
                V.tensor_tensor(Y[:, o, :], Y[:, o, :], T[:, o % 4, 0:TOK], ALU.add).then_inc(done, 1)

            def x1_rest(o):
                dve.wait_ge(x1_high, o + 1)
                V.tensor_tensor(U[:, KD + o, :], Y[:, o, :], U[:, o, :].bitcast(F32), ALU.subtract).then_inc(x1_low, 1)

            for o in range(KD):
                residual(o, G_POST0, x1_sum)
                if o:
                    x1_rest(o - 1)
            x1_rest(KD - 1)
            low(D0 + 2, 0)
            norm(2)

            later_sum, o_sum = Z[:, 1, 0], Z[:, 1, 1]

            def scaled(k, g, s):
                a_ = k * 16 + (4 * g + s)
                q = slice(FIRST_Q[s], SEQ)
                dve.wait_ge(qk_done, a_ + 1)
                if not (isinstance(a_, int) and a_ == 0):
                    dve.wait_ge(l_ready, a_)
                V.tensor_scalar(T[:, 0, q], Z[:, 0, s % 2, q], SCALE, BIAS[:, bass.ds(k * GRP + g, 1)],
                                ALU.mult, ALU.add).then_inc(z_out, 1)

            def masked_part(tile, s):
                q0 = FIRST_Q[s]
                return (tile[:, q0:q0 + 2 * P], MSK[:, :]) if s == 0 else (tile[:, q0:q0 + P], MSK[:, P:2 * P])

            def softplus(k, g, s):
                a_ = k * 16 + (4 * g + s)
                q = slice(FIRST_Q[s], SEQ)
                dve.wait_ge(l_ready, a_ + 1)
                V.scalar_tensor_tensor(T[:, 3, q], T[:, 0, q], 0.0, T[:, 1, q], ALU.min, ALU.subtract)
                steps.done(V.scalar_tensor_tensor(T[:, 2, q], T[:, 0, q], 0.0, T[:, 1, q], ALU.max, ALU.add))
                part, mask = masked_part(T[:, 2], s)
                V.tensor_tensor(part, part, mask, ALU.mult).then_inc(sp_ready, 1)

            def sp_rest(k, g, s):
                q = slice(FIRST_Q[s], SEQ)
                dve.wait_ge(sp_high, k * 16 + (4 * g + s + 1))
                V.tensor_tensor(U[:, 37, q], T[:, 2, q], U[:, 36, q].bitcast(F32), ALU.subtract).then_inc(sp_low, 1)

            def exponent(k, g, s):
                q = slice(FIRST_Q[s], SEQ)
                dve.wait_ge(later_done, k * 16 + (4 * g + s + 1))
                V.tensor_tensor(T[:, 3, q], T[:, 3, q], later_sum[:, q], ALU.subtract).then_inc(arg_ready, 1)

            def mask_weights(k, g, s):
                dve.wait_ge(at_exp, k * 16 + (4 * g + s + 1))
                part, mask = masked_part(T[:, 4], s)
                V.tensor_tensor(part, part, mask, ALU.mult).then_inc(at_masked, 1)

            def at_rest(k, g, s):
                q = slice(FIRST_Q[s], SEQ)
                dve.wait_ge(at_high, k * 16 + (4 * g + s + 1))
                V.tensor_tensor(U[:, 39, q], T[:, 4, q], U[:, 38, q].bitcast(F32), ALU.subtract).then_inc(at_low, 1)

            def head_out(k, g):
                dve.wait_ge(pv_done, k * 16 + (4 * g + 4))
                y = y_one(Y[:, bass.ds(k * GRP + g, 1), 0:SEQ])
                V.tensor_tensor(y, y, o_sum, ALU.mult).then_inc(o_out, 1)

            def pair(k, off, g=None, att=None, tail=None, gate=None, turn=False, units=True, first=False):
                for s in range(4):
                    before = (*att, s - 1) if att and s else (*tail, 3) if tail and s == 0 else None
                    if before:
                        exponent(*before)
                    if att and s == 0:
                        scaled(*att, 0)
                    if units and not (first and s < 2):
                        low(k * 20 + (D0 + off + s + 1), (s + 1) % 2)
                    if s == 0 and gate:
                        dve.wait_ge(sgb_ready, gate[0] * GRP + (gate[1] + 1))
                        y = y_one(Y[:, bass.ds(gate[0] * GRP + gate[1], 1), :])
                        V.tensor_tensor(y, y, T[:, 8, 0:TOK], ALU.mult).then_inc(silu_done, 1)
                        dve.wait_ge(silu_done, gate[0] * GRP + (gate[1] + 1))
                    if before:
                        mask_weights(*before)
                    if att:
                        softplus(*att, s)
                    if before:
                        at_rest(*before)
                    if att:
                        sp_rest(*att, s)
                        if s < 3:
                            scaled(*att, s + 1)
                    if s == 1 and tail:
                        head_out(*tail)
                    if s == 2 and units:
                        dve.wait_ge(unit_done, k * 20 + (D0 + off + 2))
                        if g is None:
                            if not first:
                                dve.wait_ge(kv_t, k * 2)
                            V.tensor_tensor(halves(T[:, 6, 0:TOK]), PS[:, 0, :, 0:HALF], halves(RS[:]), ALU.mult).then_inc(strip_out, 1)
                            dve.wait_ge(strip_out, k * 10 + (SD0 + 1))
                            steps.done(V.tensor_copy(KST[:, bass.ds(k, 1), :].rearrange("p o n -> p (o n)"), T[:, 6, SEQ:TOK]))
                        else:
                            V.tensor_tensor(T[:, 5, 0:HALF], PS[:, 0, 0, 0:HALF], RS[:, 0:HALF], ALU.mult)
                            V.tensor_tensor(T[:, 5, HALF:SEQ], PS[:, 0, 1, 0:SEQ - HALF], RS[:, HALF:SEQ], ALU.mult)
                            qs = QS[:, bass.ds(k * P, P)].rearrange("p (b g t) -> p b g t", b=NB, g=GRP)[:, :, g, :]
                            V.tensor_tensor(qs, PS[:, 0, 1, SEQ - HALF:HALF].rearrange("p (b t) -> p b t", t=NT),
                                            RS[:, SEQ:TOK].rearrange("p (b t) -> p b t", t=NT), ALU.mult).then_inc(strip_out, 1)
                    if s == 3 and g is not None and units:
                        dve.wait_ge(q_high, k * GRP + (g + 1))
                        V.tensor_tensor(U[:, 33 + 2 * (g % 2), 0:SEQ], T[:, 5, 0:SEQ],
                                        U[:, 32 + 2 * (g % 2), 0:SEQ].bitcast(F32), ALU.subtract).then_inc(q_low, 1)
                    if s == 3 and turn:
                        dve.wait_ge(v_high, k + 1)
                        V.tensor_tensor(KVP[:, 3, :], T[:, 10, 0:SEQ], KVP[:, 2, :].bitcast(F32), ALU.subtract).then_inc(v_low, 1)
                if units:
                    dve.wait_ge(unit_done, k * 20 + (D0 + off + 4))
                    to = T[:, 7, 0:TOK] if g is None else y_one(Y[:, bass.ds(k * GRP + g, 1), :])
                    V.tensor_tensor(halves(to), PS[:, 1, :, 0:HALF], halves(RS[:]), ALU.mult).then_inc(strip_out, 1)
                    if g is None:
                        dve.wait_ge(k_high, k + 1)
                        V.tensor_tensor(KVP[:, 1, :], T[:, 6, 0:SEQ], KVP[:, 0, :].bitcast(F32), ALU.subtract).then_inc(k_low, 1)

            dve.wait_ge(bias_in, 16)
            dve.wait_ge(masks, 1)
            pair(0, 0, first=True)
            dve.wait_ge(x1_kept, 16 * KD)
            pair(0, 4, g=0, turn=True)

            def group(k, whole):
                pair(k, 8, g=1, att=(k, 0), gate=(k, 0))
                pair(k, 12, g=2, att=(k, 1), tail=(k, 0), gate=(k, 1))
                pair(k, 16, g=3, att=(k, 2), tail=(k, 1), gate=(k, 2))
                if whole:
                    pair(k + 1, 0, att=(k, 3), tail=(k, 2), gate=(k, 3))
                    pair(k + 1, 4, g=0, tail=(k, 3), turn=True)

            with dve.Fori(0, NKV - 1) as k:
                steps.loop(k, 0, STEPS_D)
                group(k, True)
            steps.leave(NKV - 1)
            group(NKV - 1, False)
            pair(0, 0, att=(NKV - 1, 3), tail=(NKV - 1, 2), gate=(NKV - 1, 3), units=False)
            last_head = (NKV - 1, 3)
            exponent(*last_head, 3)
            mask_weights(*last_head, 3)
            at_rest(*last_head, 3)
            V.memset(T[:, 2, 0:SEQ], 0.0)
            dve.wait_ge(at_low, NH * 4)
            steps.done(V.memset(T[:, 4, 0:SEQ], 0.0))
            low(E0 + 1, 1)
            for k in range(NKV):
                ins = V.tensor_copy(T[:, 6, k * P:(k + 1) * P].rearrange("p (b g t) -> p b g t", b=NB, g=GRP),
                                    BIAS[:, k * GRP:(k + 1) * GRP].unsqueeze(1).unsqueeze(3).to_broadcast([P, NB, GRP, NT]))
            steps.done(ins)
            head_out(*last_head)

            def add_values(m, sequences):
                for b in sequences:
                    dve.wait_ge(d_pv_b, m * 8 + (b + 1))
                    V.tensor_tensor(value_sums(b), value_sums(b), d_bank(b)[0:QR, :], ALU.add).then_inc(d_sum_b, 1)

            def d_chain(n, par, rows):
                q = slice(0, SEQ)
                fresh = isinstance(n, int) and n == 0
                if fresh:
                    dve.wait_ge(d_z, 1)
                else:
                    dve.wait_ge(kp_used, n * 8)
                    dve.wait_ge(d_l, n)
                V.scalar_tensor_tensor(T[0:rows, 0, q], Z[0:rows, 0, par, :], SCALE, T[0:rows, 6, q],
                                       ALU.mult, ALU.add).then_inc(d_zout, 1)
                if not fresh:
                    add_values(n - 1, range(0, 4))
                dve.wait_ge(d_l, n + 1)
                steps.done(V.scalar_tensor_tensor(T[0:rows, 2, q], T[0:rows, 0, q], 0.0, T[0:rows, 1, q], ALU.max, ALU.add))
                if fresh:
                    steps.done(V.tensor_tensor(T[0:rows, 3, q], T[0:rows, 0, q], T[0:rows, 2, q], ALU.subtract))
                    dve.wait_ge(d_mask, 1)
                    V.tensor_tensor(T[0:rows, 2, q], T[0:rows, 2, q], T[0:rows, 7, q], ALU.mult).then_inc(d_sp, 1)
                else:
                    V.tensor_tensor(T[0:rows, 3, q], T[0:rows, 0, q], T[0:rows, 2, q], ALU.subtract).then_inc(d_sp, 1)
                if not fresh:
                    add_values(n - 1, range(4, 5))
                dve.wait_ge(d_high, n + 1)
                V.tensor_tensor(KVP[:, 1, :], T[:, 2, q], KVP[:, 0, :].bitcast(F32), ALU.subtract).then_inc(d_low, 1)
                if not fresh:
                    add_values(n - 1, range(5, 8))
                dve.wait_ge(d_later, n + 1)
                V.tensor_tensor(T[0:rows, 3, q], T[0:rows, 3, q], later_sum[0:rows, :], ALU.subtract).then_inc(d_arg, 1)
                if fresh:
                    dve.wait_ge(d_exp, 1)
                    V.tensor_tensor(d_weights(rows), d_weights(rows), d_columns(T[0:rows, 7, q]), ALU.mult).then_inc(d_at, 1)

            d_chain(0, 0, NS)
            dve.wait_ge(d_cleared, 1)
            with dve.Fori(0, NPAGE // 2) as i:
                steps.loop(i, 0, 2)
                for m in (1, 2):
                    n = i * 2 + m
                    for b in range(1, NB, 2):
                        dve.wait_ge(kp_t, n * 8 + (b - 7))
                        if b >= 4:
                            dve.wait_ge(kp_used, n * 8 + (b - 11))
                        V.tensor_copy(KPT[:, b % 4, :], d_bank(b)).then_inc(kp_odd, 1)
                    d_chain(n, m % 2, P)
            steps.leave(NPAGE // 2)
            add_values(NPAGE, range(NB))
            dve.wait_ge(d_turned, 1)
            for k in range(NKV):
                y = Y[:, k * GRP:(k + 1) * GRP, SEQ:TOK].rearrange("p g (b t) -> p g b t", t=NT)
                o = d_bank(k).rearrange("p (b k g t) -> p k g b t", b=NB, k=NKV, g=GRP)[:, k]
                ins = V.tensor_tensor(y, y, o, ALU.mult)
            ins.then_inc(d_out, 1)

            for o in range(KD):
                dve.wait_ge(y2_high, o + 1)
                V.tensor_tensor(U[:, KD + o, :], Y[:, o, :], U[:, o, :].bitcast(F32), ALU.subtract).then_inc(y2_low, 1)

            def pair_e(i, first, last):
                for s in range(4):
                    if not (first and s == 0) and not (last and s == 3):
                        low(i * 4 + (E0 + s + 1), (s + 1) % 2)
                    if s == 2:
                        out_tile(i * 2, i * 4 + (E0 + 2), 0, 0)
                out_tile(i * 2, i * 4 + (E0 + 4), 1, 1)

            pair_e(0, True, False)
            with dve.Fori(1, KD // 2 - 1) as i:
                pair_e(i, False, False)
            pair_e(KD // 2 - 1, False, True)
            norm(3)

            def sample_rows(o):
                dve.wait_ge(yt_done, o + 1)
                V.tensor_copy(YO[0:NS, 4, o * P:(o + 1) * P], Z[0:NS, o % 2, 1, 0:P]).then_inc(yt_out_s, 1)

            for o in range(KD):
                residual(o, G_POST1, y_sum)
                if o:
                    sample_rows(o - 1)
            sample_rows(KD - 1)



_INS = ["x_prompt", "x_sample", "cache_k", "cache_v", "state_conv", "state_h", "page_table", "g_pre", "g_post",
        "a_w_in", "a_conv_w", "a_conv_b", "a_w_r", "a_b_r", "a_w_i", "a_b_i", "a_lambda", "a_w_out", "kv_norm",
        "w_k", "w_v", "b_w_in", "b_logit", "b_w_out"]
_OUTS = [(1, SEQ, D), (NB, NT, D), (1, 1, SW, RNN), (1, 1, RNN), (1, SEQ, NKV, DH), (1, SEQ, NKV, DH),
         (NB, 1, SW, RNN), (NB, 1, RNN), (NB, NT, NKV, DH), (NB, NT, NKV, DH)]


def kernel(**inputs):
    import numpy as _np
    import concourse.bacc as _bacc
    from concourse import mybir as _mybir
    from concourse.bass_utils import run_bass_kernel_spmd as _run

    nc = _bacc.Bacc("TRN2", target_bir_lowering=False, num_devices=1)
    arrays, ins = {}, {}
    for name in _INS:
        x = _np.ascontiguousarray(inputs[name])
        arrays[f"in_{name}_dram"] = x
        ins[name] = nc.dram_tensor(f"in_{name}_dram", x.shape, _mybir.dt.from_np(x.dtype), kind="ExternalInput").ap()
    outs = [nc.dram_tensor(f"out_{i}_dram", shape, _mybir.dt.float32, kind="ExternalOutput").ap()
            for i, shape in enumerate(_OUTS)]
    build(nc, ins, outs)
    r = _run(nc, [arrays], core_ids=[0])
    return tuple(r.results[0][f"out_{i}_dram"] for i in range(len(_OUTS)))
```
